# Optimizing a Trainium2 kernel written in Bass

```python
import math
import jax, jax.numpy as jnp
from jax import lax
import numpy as np

D_MODEL = 1024
BATCH = 1
SEQ = 256
DEPTH = 2

N_A_LAYERS = DEPTH // 2
N_B_LAYERS = DEPTH - N_A_LAYERS
EPS = 1e-6

D_FF = 2816
FFN_RES = 0.5

HGRN_HEADS = 8
HGRN_EXPAND = 128
HGRN_F_DIM = HGRN_HEADS * HGRN_EXPAND
HGRN_V_HEAD = D_MODEL // HGRN_HEADS
HGRN_CHUNK = 64
HGRN_IN_DIM = 2 * HGRN_F_DIM + 2 * D_MODEL

DIFF_HEADS = 8
DIFF_HEAD_DIM = D_MODEL // (2 * DIFF_HEADS)
DIFF_V_DIM = 2 * DIFF_HEAD_DIM
DIFF_Q_DIM = 2 * DIFF_HEADS * DIFF_HEAD_DIM
DIFF_KV_DIM = 2 * DIFF_HEADS * DIFF_HEAD_DIM + DIFF_HEADS * DIFF_V_DIM
Q_BLOCK = 128

N_BUCKETS = 32
MAX_DISTANCE = 128

kernel_name = "yoco_hgrn2_diffattn_macaron"

def rmsnorm(x, w):
    xf = x.astype(jnp.float32)
    y = xf * lax.rsqrt(jnp.mean(xf * xf, axis=-1, keepdims=True) + EPS)
    return (y * w.astype(jnp.float32)).astype(x.dtype)

def swiglu(x, w_in, w_out):
    g, u = jnp.split(x @ w_in, 2, axis=-1)
    return (jax.nn.silu(g) * u) @ w_out

def to_heads(t, n_heads):
    b, s, _ = t.shape
    return t.reshape(b, s, n_heads, -1).transpose(0, 2, 1, 3)

def chunk_gated_recurrence(q, k, v, logf):
    b_, h_, s_, dk = q.shape
    dv = v.shape[-1]
    c = HGRN_CHUNK
    n = s_ // c
    q = q.reshape(b_, h_, n, c, dk)
    k = k.reshape(b_, h_, n, c, dk)
    v = v.reshape(b_, h_, n, c, dv)
    bcum = jnp.cumsum(logf.reshape(b_, h_, n, c, dk), axis=3)
    b_last = bcum[:, :, :, -1:, :]
    b_mid = bcum[:, :, :, c // 2 - 1:c // 2, :]
    u = jnp.einsum('bhncd,bhnce->bhnde', k * jnp.exp(b_last - bcum), v)
    decay = jnp.exp(b_last[:, :, :, 0, :])

    def step(s, xs):
        dec, un = xs
        return dec[..., None] * s + un, s

    s0 = jnp.zeros((b_, h_, dk, dv), jnp.float32)
    _, s_prev = lax.scan(step, s0, (jnp.moveaxis(decay, 2, 0), jnp.moveaxis(u, 2, 0)))
    s_prev = jnp.moveaxis(s_prev, 0, 2)
    o_inter = jnp.einsum('bhncd,bhnde->bhnce', q * jnp.exp(bcum), s_prev)
    qi = q * jnp.exp(bcum - b_mid)
    ki = k * jnp.exp(b_mid - bcum)
    a = jnp.einsum('bhncd,bhnmd->bhncm', qi, ki)
    mask = jnp.tril(jnp.ones((c, c), dtype=bool))
    a = jnp.where(mask, a, 0.0)
    o_intra = jnp.einsum('bhncm,bhnme->bhnce', a, v)
    return (o_inter + o_intra).reshape(b_, h_, s_, dv)

def hgrn2_mixer(h, w_in, lb, gnorm_w, w_out):
    b_, s_, _ = h.shape
    q, f, i, g = jnp.split(h @ w_in, [HGRN_F_DIM, 2 * HGRN_F_DIM, 2 * HGRN_F_DIM + D_MODEL], axis=-1)
    q = jax.nn.silu(q.astype(jnp.float32))
    f = lb + (1.0 - lb) * jax.nn.sigmoid(f.astype(jnp.float32))
    k = 1.0 - f
    o = chunk_gated_recurrence(to_heads(q, HGRN_HEADS), to_heads(k, HGRN_HEADS),
                               to_heads(i.astype(jnp.float32), HGRN_HEADS),
                               to_heads(jnp.log(f), HGRN_HEADS))
    o = o.transpose(0, 2, 1, 3)
    gate = jax.nn.silu(g.astype(jnp.float32)).reshape(b_, s_, HGRN_HEADS, HGRN_V_HEAD)
    o = rmsnorm(o, gnorm_w) * gate
    return (o.reshape(b_, s_, D_MODEL).astype(h.dtype) @ w_out).astype(h.dtype)

def t5_bucket(rel):
    n = jnp.maximum(rel, 0)
    max_exact = N_BUCKETS // 2
    nf = jnp.maximum(n, 1).astype(jnp.float32)
    large = max_exact + (jnp.log(nf / max_exact) / math.log(MAX_DISTANCE / max_exact)
                         * (N_BUCKETS - max_exact)).astype(jnp.int32)
    large = jnp.minimum(large, N_BUCKETS - 1)
    return jnp.where(n < max_exact, n, large)

def shared_kv(h, kv_norm_w, w_kv):
    kv = rmsnorm(h, kv_norm_w) @ w_kv
    hd = DIFF_HEADS * DIFF_HEAD_DIM
    k1, k2, v = jnp.split(kv, [hd, 2 * hd], axis=-1)
    return (to_heads(k1, DIFF_HEADS), to_heads(k2, DIFF_HEADS), to_heads(v, DIFF_HEADS))

def diff_attention(h, k1, k2, v, w_q, lam_p, subln_w, w_out, rel_bias, lambda_init):
    b_, s_, _ = h.shape
    scale = DIFF_HEAD_DIM ** -0.5
    q1, q2 = jnp.split(h @ w_q, 2, axis=-1)
    nb = s_ // Q_BLOCK

    def blocks(t):
        t = (to_heads(t, DIFF_HEADS) * scale).astype(h.dtype)
        return t.reshape(b_, DIFF_HEADS, nb, Q_BLOCK, DIFF_HEAD_DIM).transpose(2, 0, 1, 3, 4)

    lp = lam_p.astype(jnp.float32)
    lam = jnp.exp(jnp.sum(lp[0] * lp[1])) - jnp.exp(jnp.sum(lp[2] * lp[3])) + lambda_init
    k_pos = jnp.arange(s_, dtype=jnp.int32)
    table = rel_bias.astype(jnp.float32)

    def one_block(args):
        q1c, q2c, blk = args
        q_pos = blk * Q_BLOCK + jnp.arange(Q_BLOCK, dtype=jnp.int32)
        rel = q_pos[:, None] - k_pos[None, :]
        bias = table[t5_bucket(rel)].transpose(2, 0, 1)[None]
        causal = rel >= 0

        def probs(qc, kk):
            sc = jnp.einsum('bhqd,bhkd->bhqk', qc, kk).astype(jnp.float32) + bias
            return jax.nn.softmax(jnp.where(causal, sc, -jnp.inf), axis=-1)

        p = probs(q1c, k1) - lam * probs(q2c, k2)
        return jnp.einsum('bhqk,bhke->bhqe', p.astype(v.dtype), v)

    o = lax.map(one_block, (blocks(q1), blocks(q2), jnp.arange(nb, dtype=jnp.int32)))
    o = o.transpose(1, 0, 3, 2, 4).reshape(b_, s_, DIFF_HEADS, DIFF_V_DIM)
    o = rmsnorm(o, subln_w) * (1.0 - lambda_init)
    return (o.reshape(b_, s_, D_MODEL) @ w_out).astype(h.dtype)

def setup_inputs(seed: int = 0) -> dict:
    key = jax.random.key(seed)
    ks = jax.random.split(key, 16)
    f32 = jnp.float32

    def nrm(k, shape, fan_in):
        return jax.random.normal(k, shape, f32) * fan_in ** -0.5

    def gain(k, shape):
        return 1.0 + 0.02 * jax.random.normal(k, shape, f32)

    return {
        "x": jax.random.normal(ks[0], (BATCH, SEQ, D_MODEL), f32),
        "norm_w": gain(ks[1], (DEPTH, 3, D_MODEL)),
        "ffn_w_in": nrm(ks[2], (DEPTH, 2, D_MODEL, 2 * D_FF), D_MODEL),
        "ffn_w_out": nrm(ks[3], (DEPTH, 2, D_FF, D_MODEL), D_FF),
        "hgrn_w_in": nrm(ks[4], (N_A_LAYERS, D_MODEL, HGRN_IN_DIM), D_MODEL),
        "hgrn_lower_bounds": 0.1 * jax.random.normal(ks[5], (DEPTH, HGRN_F_DIM), f32),
        "hgrn_gnorm_w": gain(ks[6], (N_A_LAYERS, HGRN_V_HEAD)),
        "hgrn_w_out": nrm(ks[7], (N_A_LAYERS, D_MODEL, D_MODEL), D_MODEL),
        "kv_norm_w": gain(ks[8], (D_MODEL,)),
        "w_kv": nrm(ks[9], (D_MODEL, DIFF_KV_DIM), D_MODEL),
        "rel_bias": 0.5 * jax.random.normal(ks[10], (N_BUCKETS, DIFF_HEADS), f32),
        "diff_w_q": nrm(ks[11], (N_B_LAYERS, D_MODEL, DIFF_Q_DIM), D_MODEL),
        "diff_lambda": 0.1 * jax.random.normal(ks[12], (N_B_LAYERS, 4, DIFF_HEAD_DIM), f32),
        "diff_subln_w": gain(ks[13], (N_B_LAYERS, DIFF_V_DIM)),
        "diff_w_out": nrm(ks[14], (N_B_LAYERS, D_MODEL, D_MODEL), D_MODEL),
        "final_norm_w": gain(ks[15], (D_MODEL,)),
    }

def reference(x, norm_w, ffn_w_in, ffn_w_out, hgrn_w_in, hgrn_lower_bounds, hgrn_gnorm_w,
              hgrn_w_out, kv_norm_w, w_kv, rel_bias, diff_w_q, diff_lambda, diff_subln_w,
              diff_w_out, final_norm_w):
    lbs = jnp.cumsum(jax.nn.softmax(hgrn_lower_bounds.astype(jnp.float32), axis=0), axis=0)
    h = x
    k1 = k2 = v = None
    for l in range(DEPTH):
        h = h + FFN_RES * swiglu(rmsnorm(h, norm_w[l, 0]), ffn_w_in[l, 0], ffn_w_out[l, 0])
        hn = rmsnorm(h, norm_w[l, 1])
        if l < N_A_LAYERS:
            h = h + hgrn2_mixer(hn, hgrn_w_in[l], lbs[l], hgrn_gnorm_w[l], hgrn_w_out[l])
        else:
            j = l - N_A_LAYERS
            lambda_init = 0.8 - 0.6 * math.exp(-0.3 * l)
            h = h + diff_attention(hn, k1, k2, v, diff_w_q[j], diff_lambda[j], diff_subln_w[j],
                                   diff_w_out[j], rel_bias, lambda_init)
        h = h + FFN_RES * swiglu(rmsnorm(h, norm_w[l, 2]), ffn_w_in[l, 1], ffn_w_out[l, 1])
        if l == N_A_LAYERS - 1:
            k1, k2, v = shared_kv(h, kv_norm_w, w_kv)
    return rmsnorm(h, final_norm_w)


_drawn_inputs = setup_inputs


def setup_inputs(seed=0):
    import zlib

    import numpy as np

    out = dict(_drawn_inputs(seed))
    spreads = {}
    factors = {'hgrn_lower_bounds': 6.85,
     'hgrn_gnorm_w': 4.164,
     'kv_norm_w': 4.4,
     'diff_subln_w': 5.939,
     'final_norm_w': 2.862}
    for name, (base, spread) in spreads.items():
        noise = np.random.default_rng([zlib.crc32(name.encode()), seed]).standard_normal(out[name].shape)
        drawn = base * np.exp(spread * noise) if base else spread * noise
        out[name] = __import__('jax').numpy.asarray(drawn.astype(out[name].dtype))
    for name, factor in factors.items():
        out[name] = (out[name] * factor).astype(out[name].dtype)
    return out
```

```python
import math

import concourse.bass as bass
import numpy as np
from concourse import mybir
from concourse.alu_op_type import AluOpType as ALU

F32 = mybir.dt.float32
F32R = mybir.dt.float32r
U32 = mybir.dt.uint32
ACT = mybir.ActivationFunctionType
AX_X = mybir.AxisListType.X
ds = bass.ds

P = 128
EPS = 1e-6
MASKED = -3.0e38
CHUNK = 64
N_BUCKETS = 32
MAX_DISTANCE = 128
RING = 4
LOTS = 8


def shape_constants(T):
    ident = np.eye(P, dtype=np.float32)
    m, c = np.arange(P)[:, None], np.arange(P)[None, :]
    causal = ((m // CHUNK == c // CHUNK) & (m <= c)).astype(np.float32)
    resets = np.broadcast_to((np.arange(2 * T) % CHUNK != 0).astype(np.float32), (P, 2 * T))
    exact = N_BUCKETS // 2
    rel = (T - 1 - np.arange(T)).astype(np.int64)
    far = np.maximum(rel, 1).astype(np.float32)
    large = exact + (np.log(far / np.float32(exact)) / np.float32(math.log(MAX_DISTANCE / exact))
                     * np.float32(N_BUCKETS - exact)).astype(np.int32)
    bucket = np.where(rel < exact, rel, np.minimum(large, N_BUCKETS - 1))
    onehot = (np.arange(N_BUCKETS)[:, None] == bucket[None, :]).astype(np.float32)
    return {"c_ident": ident, "c_causal": causal, "c_resets": np.ascontiguousarray(resets),
            "c_onehot": onehot}


def trunk(nc, x, norm_w, ffn_w_in, ffn_w_out, hgrn_w_in, hgrn_lower_bounds, hgrn_gnorm_w,
          hgrn_w_out, kv_norm_w, w_kv, rel_bias, diff_w_q, diff_lambda, diff_subln_w,
          diff_w_out, final_norm_w, c_ident, c_causal, c_resets, c_onehot, out):
    _, T, D = x.shape
    F = ffn_w_out.shape[2]
    H = rel_bias.shape[1]
    KD, KF, TB = D // P, F // P, T // P
    NP_IN = F // 256
    NP_OUT = D // 256
    HP = H // 2
    DH = diff_lambda.shape[2]
    LAMBDA_INIT = 0.8 - 0.6 * math.exp(-0.3 * 1)
    assert T == 256 and D == 1024 and KF == 22 and H == 8 and DH == 64

    WHOLE = [(0, 4), (4, 4)]
    QUARTERS = [(0, [(0, 3), (3, 3)]), (6, [(0, 3), (3, 2)]),
                (11, [(0, 3), (3, 3)]), (17, [(0, 3), (3, 2)])]

    FFN_SLABS = 2 * NP_IN + 4 * NP_OUT
    S_FFN1 = 0
    S_HGRN = S_FFN1 + FFN_SLABS
    S_HOUT = S_HGRN + 4 * HP
    S_FFN2 = S_HOUT + NP_OUT
    S_KV = S_FFN2 + FFN_SLABS
    S_FFN3 = S_KV + 8
    S_DIFF = S_FFN3 + FFN_SLABS
    S_DOUT = S_DIFF + 4
    S_FFN4 = S_DOUT + NP_OUT
    S_END = S_FFN4 + FFN_SLABS

    W_NORM = {0: 0, 1: KD, 2: 2 * KD, 3: 3 * KD, 4: 4 * KD, 5: 5 * KD, 6: 7 * KD}
    W_KV = 6 * KD
    W_LB = 8 * KD
    W_GN = 10 * KD
    W_SUB = W_GN + 1
    NCOL = W_SUB + 1

    VECTORS = [(norm_w.rearrange("l s (c p) -> (l s c) p", p=P), 0),
               (kv_norm_w.rearrange("(c p) -> c p", p=P), W_KV),
               (final_norm_w.rearrange("(c p) -> c p", p=P), W_NORM[6]),
               (hgrn_lower_bounds.rearrange("l (c p) -> (l c) p", p=P), W_LB),
               (hgrn_gnorm_w, W_GN), (diff_subln_w, W_SUB)]

    at = [16512]

    def place(name, shape, dt, offset=None):
        size = 4 * int(np.prod(shape[1:]))
        where = at[0] if offset is None else offset
        if offset is None:
            at[0] += -(-size // 32) * 32
        return nc.alloc_sbuf_tensor_at(name, list(shape), dt, offset=where), where

    raw, _ = place("raw", [P, LOTS, 4, 256], F32)
    w_hi, _ = place("w_hi", [P, RING, 8, 256], F32R)
    w_lo, _ = place("w_lo", [P, RING, 8, 256], F32R)
    x_hi, _ = place("x_hi", [P, KD, T], F32R)
    x_lo, _ = place("x_lo", [P, KD, T], F32R)
    h_hi, at_hhi = place("h_hi", [P, KF, T], F32R)
    h_lo, at_hlo = place("h_lo", [P, KF, T], F32R)
    resid, _ = place("resid", [P, KD, T], F32)
    k_T, at_w = place("k_T", [P, 2 * HP, T], F32)
    v_all, _ = place("v_all", [P, TB, D], F32)
    kx_hi, at_z = place("kx_hi", [P, KD, T], F32R)
    kx_lo, _ = place("kx_lo", [P, KD, T], F32R)
    rstd_b, _ = place("rstd_b", [P, T], F32)
    ident, _ = place("ident", [P, P], F32)
    ones, _ = place("ones", [P, P], F32)
    sumsq, _ = place("sumsq", [P, T], F32)
    square, _ = place("square", [P, T], F32)
    diag, _ = place("diag", [P, T], F32)
    gate_s, _ = place("gate_s", [P, 2, 512], F32)
    half_out, _ = place("half_out", [P, 2, T], F32)
    cols, _ = place("cols", [P, NCOL], F32)
    small, _ = place("small", [P, 84], F32)
    assert at[0] <= 229344, at[0]
    m_sq, r_col = small[:, 0:2], small[:, 2:4]
    neg_half = small[:, 4:8]
    lb, om_lb = small[:, 8:16], small[:, 16:24]
    lam4, neg_lam = small[:, 24:28], small[:, 28:29]
    o_ss, o_ms, o_rs = small[:, 32:36], small[:, 36:40], small[:, 40:44]
    p_r2, p_rl = small[:, 52:54], small[:, 56:58]
    sub_w = small[:, 60:61]

    def neg_mx(h):
        return small[:, 44 + 4 * (h % 2):48 + 4 * (h % 2)]

    def p_sum(h):
        return small[:, 76 + 4 * (h % 2):80 + 4 * (h % 2)]

    def p_r1(h):
        base = 64 + 4 * (h // 2 % 3) + h % 2
        return small[:, base:base + 3:2]

    past_hi, past_lo = at_hhi + 4 * KD * T, at_hlo + 4 * KD * T
    PAIR_BYTES = 4 * 512

    def scratch(name, shape, offset):
        return place(name, shape, F32, offset)[0]

    x_rows = scratch("x_rows", [P, TB, D], at_z)
    vec_rows = scratch("vec_rows", [P, P], at_z + 8192)
    lam_rows = scratch("lam_rows", [P, 4, DH], at_z + 8704)
    onehot = scratch("onehot", [N_BUCKETS, T], at_z + 9728)
    table = scratch("table", [N_BUCKETS, H], at_z + 10752)
    bias_rows = scratch("bias_rows", [H, T + P], at_z + 10784)
    lb_tmp = scratch("lb_tmp", [P, 4, 8], at_z + 12384)
    causal = scratch("causal", [P, P], at_w)
    resets = scratch("resets", [P, 2 * T], at_w + 512)
    hv = scratch("hv", [P, TB, 256], at_w + 512 + PAIR_BYTES)
    hgate = scratch("hgate", [P, TB, 256], at_w + 512 + 2 * PAIR_BYTES)
    kd_rows = scratch("kd_rows", [P, TB, 2, P], at_w + 512 + 3 * PAIR_BYTES)
    a_T = scratch("a_T", [P, 2, TB, P], at_w + 512 + 4 * PAIR_BYTES)
    state = scratch("state", [P, 2, 3, P], at_w + 512 + 5 * PAIR_BYTES)
    fr, fg, kk, lg, bc, dm, dl, e0 = (
        scratch(n, [P, 2, T], at_z + j * PAIR_BYTES) for j, n in enumerate(("fr", "fg", "kk", "lg", "bc", "dm", "dl", "e0")))
    e1, e2, e3, qr, sg, qq = (
        scratch(n, [P, 2, T], past_hi + j * PAIR_BYTES) for j, n in enumerate(("e1", "e2", "e3", "qr", "sg", "qq")))
    qi, ki, kd, qe = (scratch(n, [P, 2, T], past_lo + j * PAIR_BYTES) for j, n in enumerate(("qi", "ki", "kd", "qe")))
    o_sb = scratch("o_sb", [P, TB, 2, P], past_lo + 4 * PAIR_BYTES)
    o_sq = scratch("o_sq", [P, TB, 2, P], past_lo + 5 * PAIR_BYTES)
    bias = scratch("bias", [P, H, T], at_z)
    q_T = scratch("q_T", [P, 2 * HP, T], at_z + 8192)
    NS = P + T
    sc = scratch("sc", [P, 2, 2, NS], past_hi)
    pr = scratch("pr", [P, 2, NS], past_hi + 4 * 4 * NS)
    p_T = scratch("p_T", [P, 2, NS], past_lo)
    y_rows = scratch("y_rows", [P, TB, D], at_z)
    y_w = scratch("y_w", [P, KD, T], at_w)

    banks = [nc.alloc_psum_tensor(f"bank{b}", [P, 512], F32) for b in range(8)]
    bias_dram = nc.dram_tensor("bias_scratch", [H, T + P], F32, kind="Internal")
    bias_wide = nc.dram_tensor("bias_wide", [P, H * (T + P)], F32, kind="Internal")

    def sem(name):
        return nc.alloc_semaphore(name)

    lot_landed = [sem(f"lot_landed{j}") for j in range(LOTS)]
    hi_split, lo_split, slab_used = sem("hi_split"), sem("lo_split"), sem("slab_used")
    x_landed = [sem(f"x_landed{j}") for j in range(2)]
    vec_landed = [sem("vec_landed_sp"), sem("vec_landed_act")]
    ident_landed, hg_landed = sem("ident_landed"), sem("hg_landed")
    tab_landed, lam_landed = sem("tab_landed"), sem("lam_landed")
    ones_set, neg_set, aT_zeroed, brow_set = sem("ones_set"), sem("neg_set"), sem("aT_zeroed"), sem("brow_set")
    x_turned, vec_turned, cols_ready = sem("x_turned"), sem("vec_turned"), sem("cols_ready")
    brow_done, brow_ready, bias_stored, bias_widened, bias_landed = (
        sem("brow_done"), sem("brow_ready"), sem("bias_stored"), sem("bias_widened"), sem("bias_landed"))
    lb_step, lb_exp, lam_dot, lam_exp, lam_step = (
        sem("lb_step"), sem("lb_exp"), sem("lam_dot"), sem("lam_exp"), sem("lam_step"))
    resid_act = sem("resid_act")
    even_done, half_ready, resid_ready = sem("even_done"), sem("half_ready"), sem("resid_ready")
    xh_ready, xl_ready, kxh_ready, kxl_ready = (
        sem("xh_ready"), sem("xl_ready"), sem("kxh_ready"), sem("kxl_ready"))
    sumsq_step, stat_done, ms_ready, rstd_ready, diag_ready, rb_done, rb_ready = (
        sem("sumsq_step"), sem("stat_done"), sem("ms_ready"), sem("rstd_ready"), sem("diag_ready"),
        sem("rb_done"), sem("rb_ready"))
    gate_scaled, silu_ready, hid_ready, hidh_ready, hidl_ready = (
        sem("gate_scaled"), sem("silu_ready"), sem("hid_ready"), sem("hidh_ready"), sem("hidl_ready"))
    fr_ready, fsig_ready, f_ready, lg_ready, bc_ready, d_ready, k_ready = (
        sem("fr_ready"), sem("fsig_ready"), sem("f_ready"), sem("lg_ready"), sem("bc_ready"), sem("d_ready"), sem("k_ready"))
    qr_ready, qsig_ready, q_ready = sem("qr_ready"), sem("qsig_ready"), sem("q_ready")
    e_ready, ki_ready, kqi_ready, qe_ready = sem("e_ready"), sem("ki_ready"), sem("kqi_ready"), sem("qe_ready")
    coreA_done, kdr_ready, aT_ready, coreB_done, st_ready = (
        sem("coreA_done"), sem("kdr_ready"), sem("aT_ready"), sem("coreB_done"), sem("st_ready"))
    hv_ready, gsig_ready, hgate_ready = sem("hv_ready"), sem("gsig_ready"), sem("hgate_ready")
    o_done, o_ready, osq_ready, oss_ready, oms_ready, ors_ready, on_step = (
        sem("o_done"), sem("o_ready"), sem("osq_ready"), sem("oss_ready"), sem("oms_ready"), sem("ors_ready"), sem("on_step"))
    oT_done, oh_ready, ol_ready = sem("oT_done"), sem("oh_ready"), sem("ol_ready")
    kv_ready, qT_ready = sem("kv_ready"), sem("qT_ready")
    sc_done, sc_ready, nmx_ready, exp_ready, rcp_ready, rl_ready, pr_ready, pT_done, pT_ready = (
        sem("sc_done"), sem("sc_ready"), sem("nmx_ready"), sem("exp_ready"), sem("rcp_ready"), sem("rl_ready"),
        sem("pr_ready"), sem("pT_done"), sem("pT_ready"))
    yw_ready, y_turned, y_stored = sem("yw_ready"), sem("y_turned"), sem("y_stored")
    y_ready = [sem(f"y_ready{tb}") for tb in range(TB)]

    def fh(pair):
        return 2 * (pair % 2), 2 * (pair % 2) + 1

    def u_of(head, c):
        j = (c // 2) * 2 + head
        return banks[6 + c % 2][:, j * P:(j + 1) * P]

    def out_bank(m, c):
        return ((0, 1, 2, 3, 5, 6, 4, 7), (0, 1, 2, 3, 4, 6, 5, 7))[m][c]

    def q_bank(j):
        return (0, 1, 6, 7)[j]

    def kv_bank(j):
        return (0, 1, 6, 7, 2, 3, 6, 7)[j]

    def turn_bank(m):
        return banks[(7, 5)[m]]

    block = nc.Block()
    block.__enter__()

    @block.sync
    def _(sp):
        def lot(s, i, b, src):
            m = 2 * s + b
            kc = src.shape[1]
            if m >= LOTS:
                sp.wait_ge(lo_split, m - LOTS + 1 + 8 * i)
            sp.dma_start(raw[:, m % LOTS, 0:kc, :], src).then_inc(lot_landed[m % LOTS], 16)

        def slab(s, i, w, k_first, lots, col):
            for b, (k0, kc) in enumerate(lots):
                lot(s, i, b, w[:, k_first + k0:k_first + k0 + kc, ds(col, 256)])

        def ffn(base, l, j):
            win = ffn_w_in[l, j].rearrange("(k p) n -> p k n", p=P)
            wout = ffn_w_out[l, j].rearrange("(k p) n -> p k n", p=P)

            def pair(s, i, col):
                slab(s, i, win, 0, WHOLE, col)
                slab(s + 1, i, win, 0, WHOLE, col + F)

            start = 0
            if base == 0:
                pair(0, 0, 0)
                slab(2, 0, win, 0, WHOLE, 256)
                sp.dma_start(table[:], rel_bias).then_inc(tab_landed, 16)
                sp.dma_start(onehot[:], c_onehot).then_inc(tab_landed, 16)
                sp.dma_start(lam_rows[:], diff_lambda[0].partition_broadcast(P)).then_inc(lam_landed, 16)
                sp.dma_start(causal[:], c_causal).then_inc(hg_landed, 16)
                sp.dma_start(resets[:], c_resets).then_inc(hg_landed, 16)
                slab(3, 0, win, 0, WHOLE, 256 + F)
                start = 2
            loops = (NP_IN - start) // 2
            with sp.Fori(0, loops) as i:
                pair(base + 2 * start, i, i * 512 + start * 256)
                pair(base + 2 * start + 2, i, i * 512 + (start + 1) * 256)
            if start + 2 * loops < NP_IN:
                pair(base + 2 * NP_IN - 2, 0, (NP_IN - 1) * 256)
            with sp.Fori(0, NP_OUT) as i:
                for q, (k_first, lots) in enumerate(QUARTERS):
                    slab(base + 2 * NP_IN + q, i, wout, k_first, lots, i * 256)

        for half in range(2):
            sp.dma_start(x_rows[:, :, half * 512:(half + 1) * 512],
                         x[0].rearrange("(b p) d -> p b d", p=P)[:, :, half * 512:(half + 1) * 512]
                         ).then_inc(x_landed[half], 16)
        for v, row in VECTORS[::2]:
            sp.dma_start(vec_rows[row:row + v.shape[0], :], v).then_inc(vec_landed[0], 16)
        ffn(S_FFN1, 0, 0)
        wh = hgrn_w_in[0].rearrange("(k p) n -> p k n", p=P)
        for hp in range(HP):
            for q, col in enumerate((D, 0, 2 * D, 3 * D)):
                slab(S_HGRN + 4 * hp + q, 0, wh, 0, WHOLE, col + hp * 256)
        who = hgrn_w_out[0].rearrange("(k p) n -> p k n", p=P)
        for dp in range(NP_OUT):
            slab(S_HOUT + dp, 0, who, 0, WHOLE, dp * 256)
        ffn(S_FFN2, 0, 1)
        wkv = w_kv.rearrange("(k p) n -> p k n", p=P)
        with sp.Fori(0, 2) as i:
            for q in range(4):
                slab(S_KV + q, i, wkv, 0, WHOLE, i * D + q * 256)
        ffn(S_FFN3, 1, 0)
        wq = diff_w_q[0].rearrange("(k p) n -> p k n", p=P)
        for j, col in enumerate((0, 512, 256, 768)):
            slab(S_DIFF + j, 0, wq, 0, WHOLE, col)
        wdo = diff_w_out[0].rearrange("(k p) n -> p k n", p=P)
        for dp in range(NP_OUT):
            slab(S_DOUT + dp, 0, wdo, 0, WHOLE, dp * 256)
        ffn(S_FFN4, 1, 1)
        for j in range(4):
            half, tb = divmod(j, 2)
            sp.wait_ge(y_ready[tb], half + 1)
            sp.dma_start(out[0, tb * P:(tb + 1) * P, half * 512:(half + 1) * 512],
                         y_rows[:, tb, half * 512:(half + 1) * 512]).then_inc(y_stored, 16)
        sp.wait_ge(y_stored, 64)

    @block.tensor
    def _(pe):
        mm = nc.tensor.matmul

        def three(o, whi, wlo, xhi, xlo, first, last):
            mm(o, whi, xhi, start=first, stop=False)
            mm(o, whi, xlo, start=False, stop=False)
            return mm(o, wlo, xhi, start=False, stop=last)

        def split_wait(s, i, b):
            pe.wait_ge(lo_split, 2 * s + b + 1 + 8 * i)

        def group(s, i, g, ks, out, ahi, alo, k_first=0, first=True, last=True):
            wc = slice(g * P, (g + 1) * P)
            for k in ks:
                ins = three(out, w_hi[:, s % RING, k, wc], w_lo[:, s % RING, k, wc],
                            ahi[:, k_first + k, :], alo[:, k_first + k, :],
                            first and k == ks[0], last and k == ks[-1])
            return ins

        def features(s, i, lots, outs, ahi, alo, k_first=0, first=True, last=True, middle=None):
            for b, (k0, kc) in enumerate(lots):
                split_wait(s, i, b)
                ins = group(s, i, 0, range(k0, k0 + kc), outs[0], ahi, alo, k_first, first and b == 0,
                            last and b == len(lots) - 1)
            if middle is not None:
                ins.then_inc(middle, 1)
            group(s, i, 1, range(lots[-1][0] + lots[-1][1]), outs[1], ahi, alo, k_first, first, last).then_inc(slab_used, 1)

        def two_slabs(s, bank_a, bank_b, ahi, alo, chunk_ready, count, stat_step, spread_step, together=True):
            def g0(j, ks):
                for k in ks:
                    if k % 4 == 0:
                        split_wait(s + j, 0, k // 4)
                    if j == 0:
                        pe.wait_ge(chunk_ready, count + k + 1)
                    group(s + j, 0, 0, [k], (bank_a, bank_b)[j][:, 0:T], ahi, alo, first=k == 0, last=k == KD - 1)

            if together:
                for ks in (range(KD - 2), range(KD - 2, KD)):
                    for j in range(2):
                        g0(j, ks)
                stat_step()
            else:
                g0(0, range(KD))
            group(s, 0, 1, range(KD), bank_a[:, T:2 * T], ahi, alo).then_inc(slab_used, 1)
            if together:
                spread_step()
            else:
                stat_step()
                g0(1, range(KD))
            group(s + 1, 0, 1, range(KD), bank_b[:, T:2 * T], ahi, alo).then_inc(slab_used, 1)
            if not together:
                spread_step()

        def tokens(s, i, bank, ahi, alo):
            for tb in range(TB):
                for b, (k0, kc) in enumerate(WHOLE):
                    if tb == 0:
                        split_wait(s, i, b)
                    for k in range(k0, k0 + kc):
                        t = slice(tb * P, (tb + 1) * P)
                        o = bank[:, tb * 256:(tb + 1) * 256]
                        mm(o, ahi[:, k, t], w_hi[:, s % RING, k, :], start=k == 0, stop=False)
                        mm(o, alo[:, k, t], w_hi[:, s % RING, k, :], start=False, stop=False)
                        ins = mm(o, ahi[:, k, t], w_lo[:, s % RING, k, :], start=False, stop=k == KD - 1)
            ins.then_inc(slab_used, 1)

        def two(bank):
            return [bank[:, 0:T], bank[:, T:2 * T]]

        def stat(r):
            pe.wait_ge(sumsq_step, (2 * KD - 1) * r - (r == 6))
            for tb in range(TB):
                for part in (sumsq, square)[:1 + (r == 6)]:
                    ins = mm(banks[4][:, tb:tb + 1], part[:, tb * P:(tb + 1) * P], ones[:, 0:1],
                             start=part is sumsq, stop=part is square or r < 6)
            ins.then_inc(stat_done, 1)

        def spread(r):
            pe.wait_ge(diag_ready, r + 1)
            mm(banks[5][:, 0:T], ones[:], diag[:], start=True, stop=True).then_inc(rb_done, 1)

        def bias_row():
            pe.wait_ge(tab_landed, 32)
            mm(banks[3][0:H, 0:T], table[:], onehot[:], start=True, stop=True).then_inc(brow_done, 1)

        def ffn(base, f, r_in, r_out, stats):
            def pair(s, i, p):
                g_bank, u_bank = fh(p)
                if p >= 2 or not isinstance(i, int):
                    pe.wait_ge(gate_scaled, NP_IN * f + p - 1 + 2 * i)
                features(s, i, WHOLE, two(banks[g_bank]), x_hi, x_lo)
                if p >= 2 or not isinstance(i, int):
                    pe.wait_ge(hid_ready, NP_IN * f + p - 1 + 2 * i)
                features(s + 1, i, WHOLE, two(banks[u_bank]), x_hi, x_lo)

            if stats:
                two_slabs(base, banks[0], banks[1], x_hi, x_lo, xl_ready, 8 * r_in,
                          (lambda: stat(r_in)) if r_in else bias_row, lambda: spread(r_in), together=False)
            else:
                pair(base, 0, 0)
            if r_in == 0:
                pe.wait_ge(brow_ready, 1)
            pair(base + 2, 0, 1)
            with pe.Fori(0, 4) as i:
                pair(base + 4, i, 2)
                pair(base + 6, i, 3)
            pair(base + 20, 0, 10)
            sb = base + 2 * NP_IN

            def out_pair(s, i, c, wait):
                if wait:
                    pe.wait_ge(resid_ready, 8 * r_out + c + 1 - 4 + 1 + 2 * i)
                b = [banks[4 + c % 4][:, 0:T], banks[4 + (c + 1) % 4][:, 0:T]]
                for q, (k_first, lots) in enumerate(QUARTERS):
                    pe.wait_ge(hidl_ready, NP_IN * f + (NP_IN if q == 3 else NP_IN - 1))
                    features(s + q, i, lots, b, h_hi, h_lo, k_first=k_first, first=q == 0,
                             last=q == 3, middle=even_done if q == 3 else None)

            out_pair(sb, 0, 0, False)
            out_pair(sb + 4, 0, 2, False)
            out_pair(sb + 8, 0, 4, True)
            out_pair(sb + 12, 0, 6, True)

        def out_part(base, m, dp, g, k0, k1):
            o = banks[out_bank(m, 2 * dp + g)][:, 0:T]
            for k in range(k0, k1):
                if g == 0 and k % 4 == 0:
                    split_wait(base + dp, 0, k // 4)
                if g == 0:
                    pe.wait_ge(ol_ready, HP * m + k // 2 + 1)
                wc = slice(g * P, (g + 1) * P)
                ring = (base + dp) % RING
                ins = three(o, w_hi[:, ring, k, wc], w_lo[:, ring, k, wc], h_hi[:, k, :], h_lo[:, k, :],
                            k == 0, k == KD - 1)
            if k1 == KD:
                ins.then_inc(slab_used if g else even_done, 1)

        def mixer_out(base, m):
            for dp in range(NP_OUT):
                for g in range(2):
                    out_part(base, m, dp, g, KD - 2 if 2 * dp + g < (7, 6)[m] else 0, KD)

        def turn_out(m, p):
            pe.wait_ge(on_step, (2 * (p + 1) if m == 0 else 2 * HP + p + 1))
            for head in range(2):
                for tb in range(TB):
                    ins = nc.tensor.transpose(turn_bank(m)[:, head * T + tb * P:head * T + (tb + 1) * P],
                                              o_sb[:, tb, head, :], ident[:])
            ins.then_inc(oT_done, 1)

        pe.wait_ge(ident_landed, 16)
        for c in range(KD):
            if c == 2:
                for q in range(2):
                    pe.wait_ge(vec_landed[q], 16 * 3)
                nc.tensor.transpose(banks[0][:, 0:NCOL], vec_rows[0:NCOL, :], ident[0:NCOL, 0:NCOL]).then_inc(vec_turned, 1)
            if c % 4 == 0:
                pe.wait_ge(x_landed[c // 4], 16)
            for tb in range(TB):
                ins = nc.tensor.transpose(banks[4 + c // 2][:, (c % 2) * T + tb * P:(c % 2) * T + (tb + 1) * P],
                                          x_rows[:, tb, c * P:(c + 1) * P], ident[:])
            if c % 2:
                ins.then_inc(x_turned, 1)
        pe.wait_ge(ones_set, 1)
        pe.wait_ge(cols_ready, 1)

        ffn(S_FFN1, 0, 0, 1, True)

        def core_a(i, after=True):
            pe.wait_ge(kqi_ready, i + 1)
            pe.wait_ge(ki_ready, i + 1)
            if after:
                pe.wait_ge(o_ready, i)
            for tb in range(TB):
                for head in range(2):
                    nc.tensor.transpose(banks[4][:, (2 * tb + head) * P:(2 * tb + head + 1) * P],
                                        kd[:, head, tb * P:(tb + 1) * P], ident[:])
            for head in range(2):
                for tb in range(TB):
                    t = slice(tb * P, (tb + 1) * P)
                    ins = mm(banks[5][:, (2 * head + tb) * P:(2 * head + tb + 1) * P], ki[:, head, t],
                             qi[:, head, t], start=True, stop=True)
            ins.then_inc(coreA_done, 1)

        def core_b(i):
            pe.wait_ge(kdr_ready, i + 1)
            pe.wait_ge(hv_ready, i + 1)
            for head in range(2):
                for c in range(3):
                    tok = slice(CHUNK * (c % 2), CHUNK * (c % 2) + CHUNK)
                    ins = mm(u_of(head, c), kd_rows[tok, c // 2, head, :],
                             hv[tok, c // 2, head * P:(head + 1) * P], start=True, stop=True)
            ins.then_inc(coreB_done, 1)

        def core_c(i):
            pe.wait_ge(aT_ready, i + 1)
            pe.wait_ge(qe_ready, i + 1)
            pe.wait_ge(st_ready, 6 * (i + 1))
            for tb in range(TB):
                for head in range(2):
                    lo = (2 * tb + head) * P
                    ins = mm(banks[4][:, lo:lo + P], a_T[:, head, tb, :], hv[:, tb, head * P:(head + 1) * P],
                             start=True, stop=tb == 0)
                    for c in (2 * tb, 2 * tb + 1):
                        if c:
                            rows = slice(CHUNK * (c % 2), CHUNK * (c % 2) + CHUNK)
                            ins = mm(banks[4][rows, lo:lo + P], qe[:, head, c * CHUNK:(c + 1) * CHUNK],
                                     state[:, head, c - 1, :], start=False, stop=True, skip_group_check=tb == 0)
            ins.then_inc(o_done, 1)

        two_slabs(S_HGRN, banks[0], banks[1], x_hi, x_lo, xl_ready, 8 * 1, lambda: stat(1), lambda: spread(1))
        tokens(S_HGRN + 2, 0, banks[2], x_hi, x_lo)
        tokens(S_HGRN + 3, 0, banks[3], x_hi, x_lo)
        pe.wait_ge(fr_ready, 1)
        features(S_HGRN + 4, 0, WHOLE, two(banks[0]), x_hi, x_lo)
        core_a(0, after=False)

        def head_pair(s, i, n, last):
            pe.wait_ge(qr_ready, i + n)
            features(s + 1, i, WHOLE, two(banks[1]), x_hi, x_lo)
            core_b(i + n - 1)
            tokens(s + 2, i, banks[2], x_hi, x_lo)
            core_c(i + n - 1)
            pe.wait_ge(hgate_ready, i + n)
            tokens(s + 3, i, banks[3], x_hi, x_lo)
            if not last:
                pe.wait_ge(fr_ready, i + n + 1)
                features(s + 4, i, WHOLE, two(banks[0]), x_hi, x_lo)
                turn_out(0, i + n - 1)
                core_a(i + n)

        with pe.Fori(0, HP - 2) as i:
            head_pair(S_HGRN + 4, i, 1, False)
        last = HP - 1
        head_pair(S_HGRN + 4 * last, 0, last, True)
        pe.wait_ge(qr_ready, HP)
        out_part(S_HOUT, 0, 0, 0, 0, KD - 4)
        turn_out(0, last - 1)
        out_part(S_HOUT, 0, 0, 1, 0, KD - 4)
        core_a(last)
        pe.wait_ge(hv_ready, HP)
        out_part(S_HOUT, 0, 1, 0, 0, KD - 4)
        for g in range(2):
            out_part(S_HOUT, 0, 0, g, KD - 4, KD - 2)
        core_b(last)
        out_part(S_HOUT, 0, 1, 0, KD - 4, KD - 2)
        pe.wait_ge(hgate_ready, HP)
        out_part(S_HOUT, 0, 1, 1, 0, KD - 4)
        core_c(last)
        out_part(S_HOUT, 0, 1, 1, KD - 4, KD - 2)
        for g in range(2):
            out_part(S_HOUT, 0, 2, g, 0, KD - 2)
        turn_out(0, last)
        pe.wait_ge(o_ready, HP)
        out_part(S_HOUT, 0, 3, 0, 0, KD - 2)
        mixer_out(S_HOUT, 0)

        ffn(S_FFN2, 1, 2, 3, True)

        two_slabs(S_KV, banks[0], banks[1], kx_hi, kx_lo, kxl_ready, 0, lambda: stat(3), lambda: spread(3))
        pe.wait_ge(xl_ready, 8 * 4)
        for j in range(2, 8):
            if j >= 6:
                pe.wait_ge(kv_ready, j - 3)
            if j < 4:
                features(S_KV + j, 0, WHOLE, two(banks[kv_bank(j)]), kx_hi, kx_lo)
            else:
                tokens(S_KV + j, 0, banks[kv_bank(j)], kx_hi, kx_lo)
        pe.wait_ge(kv_ready, 6)
        ffn(S_FFN3, 2, 3, 4, False)


        def scores(h):
            pe.wait_ge(qT_ready, 2 if h < 4 else 4)
            if h >= 2:
                pe.wait_ge(sc_ready, 4 * (h - 1))
            rows = slice(DH * (h % 2), DH * (h % 2) + DH)
            for m in range(2):
                bank = banks[2 * (h % 2) + m]
                n = m * HP + h // 2
                mm(bank[:, 0:P], q_T[rows, n, 0:P], k_T[rows, n, 0:P], start=True, stop=True)
                ins = mm(bank[:, P:NS], q_T[rows, n, P:T], k_T[rows, n, 0:T], start=True, stop=True)
            ins.then_inc(sc_done, 1)

        def turn_probs(h):
            pe.wait_ge(pr_ready, 2 * (h + 1))
            if h:
                pe.wait_ge(pT_ready, h)
            for j in range(3):
                ins = nc.tensor.transpose(banks[4][:, j * P:(j + 1) * P], pr[:, h % 2, j * P:(j + 1) * P], ident[:])
            ins.then_inc(pT_done, 1)

        def values(h):
            pe.wait_ge(pT_ready, h + 1)
            if h % 2 == 0:
                if h < 4:
                    pe.wait_ge(qT_ready, 3 + h // 2)
                else:
                    pe.wait_ge(o_ready, HP + h // 2 - 1)
            bank = banks[6 + (h // 2) % 2]
            vc = slice(h * P, (h + 1) * P)
            o0, o1 = (bank[:, (2 * tb + h % 2) * P:(2 * tb + h % 2 + 1) * P] for tb in range(2))
            mm(o0, p_T[:, h % 2, 0:P], v_all[:, 0, vc], start=True, stop=True)
            mm(o1, p_T[:, h % 2, P:2 * P], v_all[:, 0, vc], start=True, stop=False)
            ins = mm(o1, p_T[:, h % 2, 2 * P:NS], v_all[:, 1, vc], start=False, stop=True)
            if h % 2:
                ins.then_inc(o_done, 1)

        two_slabs(S_DIFF, banks[q_bank(0)], banks[q_bank(1)], x_hi, x_lo, xl_ready, 8 * 4,
                  lambda: stat(4), lambda: spread(4))
        for j in (2, 3):
            features(S_DIFF + j, 0, WHOLE, two(banks[q_bank(j)]), x_hi, x_lo)
            if j == 2:
                scores(0)
                scores(1)
        for h in range(H):
            if h + 2 < H:
                scores(h + 2)
            if h == H - 1:
                pe.wait_ge(sc_ready, 4 * (H - 1))
                for g in range(2):
                    out_part(S_DOUT, 1, 0, g, 0, 2)
            turn_probs(h)
            if h:
                values(h - 1)
            if h % 2 and h >= 5:
                turn_out(1, h // 2 - 2)
        pe.wait_ge(sc_ready, 4 * H)
        parts = [(dp, g) for dp in range(NP_OUT - 1) for g in range(2)]
        for k in range(0, KD - 2, 2):
            for j, (dp, g) in enumerate(parts):
                if k == 0 and out_bank(1, 2 * dp + g) == 6:
                    pe.wait_ge(o_ready, 2 * HP - 1)
                if k or dp:
                    out_part(S_DOUT, 1, dp, g, k, k + 2)
                if k == 0 and j == 3:
                    values(H - 1)
                if k == 2 and j == 2:
                    turn_out(1, HP - 2)
                if k == 4 and j == 3:
                    turn_out(1, HP - 1)
        mixer_out(S_DOUT, 1)

        ffn(S_FFN4, 3, 5, 6, True)

        for c in range(KD):
            pe.wait_ge(yw_ready, c + 1)
            for tb in range(TB):
                bank = banks[2 * tb + c // 4]
                ins = nc.tensor.transpose(bank[:, (c % 4) * P:(c % 4 + 1) * P], y_w[:, c, tb * P:(tb + 1) * P], ident[:])
        ins.then_inc(y_turned, 1)
        stat(6)

    @block.scalar
    def _(act):
        A = nc.scalar.activation

        def split(s, i, lots):
            for b, (k0, kc) in enumerate(lots):
                split_lot(2 * s + b, i, k0, kc)

        def split_lot(m, i, k0, kc):
            s = m // 2
            act.wait_ge(lot_landed[m % LOTS], 16 * (m // LOTS + 1) + 16 * i)
            if m % 2 == 0 and s >= RING:
                act.wait_ge(slab_used, s - RING + 1 + 4 * i)
            A(w_hi[:, s % RING, k0:k0 + kc, :], raw[:, m % LOTS, 0:kc, :], ACT.Copy).then_inc(hi_split, 1)

        def x_high(r, c, i=0, f=1):
            act.wait_ge(resid_ready, 8 * r + c + 1 + f * i)
            cc = c + f * i
            if r == 3:
                A(kx_hi[:, ds(cc, 1), :], resid[:, ds(cc, 1), :], ACT.Copy,
                  scale=cols[:, ds(cc + W_KV, 1)]).then_inc(kxh_ready, 1)
            A(x_hi[:, ds(cc, 1), :], resid[:, ds(cc, 1), :], ACT.Copy,
              scale=cols[:, ds(cc + W_NORM[r], 1)]).then_inc(xh_ready, 1)

        def ffn(base, f, r_out):
            def pair(s, i, p, lots_g=WHOLE, lots_u=WHOLE):
                split(s + 4, i, lots_g)
                act.wait_ge(gate_scaled, NP_IN * f + p + 1 + 2 * i)
                A(gate_s[:, p % 2, :], gate_s[:, p % 2, :], ACT.Silu).then_inc(silu_ready, 1)
                split(s + 5, i, lots_u)
                act.wait_ge(hid_ready, NP_IN * f + p + 1 + 2 * i)
                A(h_hi[:, ds(2 * p + 4 * i, 2), :], gate_s[:, p % 2, :].rearrange("p (c t) -> p c t", c=2),
                  ACT.Copy).then_inc(hidh_ready, 1)

            pair(base, 0, 0)
            with act.Fori(0, 4) as i:
                pair(base + 2, i, 1)
                pair(base + 4, i, 2)
            pair(base + 18, 0, 9, QUARTERS[0][1], QUARTERS[1][1])
            pair(base + 20, 0, 10, QUARTERS[2][1], QUARTERS[3][1])
            sb = base + 2 * NP_IN

            def out_pair(s, i, dp, lots4):
                for q in range(3):
                    if lots4[q]:
                        split(s + 4 + q, i, lots4[q])
                for g in range(2):
                    if r_out < 6:
                        x_high(r_out, 2 * dp + g, i, 2)
                if lots4[3]:
                    split(s + 7, i, lots4[3])

            with act.Fori(0, NP_OUT - 1) as i:
                out_pair(sb, i, 0, [q[1] for q in QUARTERS])
            nxt = sb + 4 * NP_OUT
            out_pair(nxt - 4, 0, NP_OUT - 1, [WHOLE if nxt + q < S_END else None for q in range(4)])

        def mixer_out(base, r_out):
            for c in range(KD):
                x_high(r_out, c)
                if c == KD - 3:
                    split(base + RING, 0, WHOLE)
            for q in range(1, RING):
                split(base + RING + q, 0, WHOLE)

        def o_square(n):
            act.wait_ge(o_ready, n)
            A(o_sq[:], o_sb[:], ACT.Square).then_inc(osq_ready, 1)

        def o_high(m, n, p, w):
            act.wait_ge(oT_done, n)
            A(h_hi[:, ds(2 * p, 2), :], turn_bank(m)[:].rearrange("p (c t) -> p c t", c=2), ACT.Copy,
              scale=w).then_inc(oh_ready, 1)

        def x_first(c):
            A(x_hi[:, c, :], resid[:, c, :], ACT.Copy,
              scale=cols[:, c + W_NORM[0]:c + W_NORM[0] + 1]).then_inc(xh_ready, 1)

        def resid_chunks(j):
            act.wait_ge(x_turned, j + 1)
            for c in (2 * j, 2 * j + 1):
                A(resid[:, c, :], banks[4 + j][:, (c % 2) * T:(c % 2 + 1) * T], ACT.Copy).then_inc(resid_act, 1)

        def x_own(j):
            for c in (2 * j, 2 * j + 1):
                act.wait_ge(resid_act, c // 4 * 2 + c % 2 + 1)
                x_first(c)

        act.dma_start(ident[:], c_ident).then_inc(ident_landed, 16)
        for v, row in VECTORS[1::2]:
            act.dma_start(vec_rows[row:row + v.shape[0], :], v).then_inc(vec_landed[1], 16)
        act.wait_ge(ones_set, 1)
        A(small[:, 61:62], ones[:, 0:1], ACT.Copy)
        act.wait_ge(cols_ready, 1)
        act.wait_ge(resid_ready, 2)
        x_first(0)
        act.wait_ge(resid_ready, 4)
        x_first(1)
        resid_chunks(1)
        split_lot(0, 0, 0, 4)
        x_own(1)
        resid_chunks(3)
        act.wait_ge(resid_ready, 8)
        x_first(4)
        x_first(5)
        split_lot(1, 0, 4, 4)
        x_own(3)
        split(1, 0, WHOLE)
        for tb in range(TB):
            ins = A(x_rows[:, tb, :], x_rows[:, tb, :], ACT.Square, accum_out=m_sq[:, tb:tb + 1])
        ins.then_inc(stat_done, 1)
        for s in range(2, 4):
            split(s, 0, WHOLE)
        act.wait_ge(lb_step, 2)
        A(lb_tmp[:, 2:4, :], lb_tmp[:, 0:2, :], ACT.Exp).then_inc(lb_exp, 1)
        act.wait_ge(lam_dot, 1)
        A(lam4[:, 2:4], lam4[:, 0:2], ACT.Exp).then_inc(lam_exp, 1)
        act.wait_ge(brow_ready, 1)
        act.wait_ge(brow_set, 1)
        act.dma_start(bias_dram[:, :], bias_rows[:]).then_inc(bias_stored, 16)

        ffn(S_FFN1, 0, 1)

        act.wait_ge(bias_stored, 16)
        act.dma_start(bias_wide[:, :], bias_dram.ap().rearrange("h r -> (h r)").partition_broadcast(P)
                      ).then_inc(bias_widened, 16)

        def head_pair(s, i, prev, first):
            n = i + (0 if first else prev + 1)
            split(s + 4, i, WHOLE)
            act.wait_ge(fr_ready, n + 1)
            A(fg[:], fr[:], ACT.Sigmoid).then_inc(fsig_ready, 1)
            split(s + 5, i, WHOLE)
            act.wait_ge(qr_ready, n + 1)
            A(sg[:], qr[:], ACT.Sigmoid).then_inc(qsig_ready, 1)
            act.wait_ge(f_ready, n + 1)
            A(lg[:], fg[:], ACT.Ln).then_inc(lg_ready, 1)
            act.wait_ge(d_ready, n + 1)
            A(e2[:], dm[:], ACT.Exp, scale=-1.0).then_inc(e_ready, 1)
            A(e3[:], dl[:], ACT.Exp).then_inc(e_ready, 1)
            A(e1[:], dm[:], ACT.Exp).then_inc(e_ready, 1)
            if not first:
                act.wait_ge(qe_ready, i + prev + 1)
            A(e0[:], bc[:], ACT.Exp).then_inc(e_ready, 1)
            if not first:
                o_square(i + prev + 1)
            split(s + 6, i, WHOLE)
            split(s + 7, i, WHOLE)
            act.wait_ge(slab_used, s + 4 + 4 * i)
            if not first:
                act.wait_ge(on_step, 2 * (i + prev + 1))
            for tb in range(TB):
                ins = A(hgate[:, tb, :], banks[3][:, tb * 256:(tb + 1) * 256], ACT.Sigmoid, scale=r_col[:, tb:tb + 1])
            ins.then_inc(gsig_ready, 1)
            if not first:
                o_high(0, i + prev + 1, i + prev, cols[:, W_GN:W_GN + 1])

        head_pair(S_HGRN, 0, -1, True)
        with act.Fori(0, HP - 1) as i:
            head_pair(S_HGRN + 4, i, 0, False)
        o_square(HP)
        o_high(0, HP, HP - 1, cols[:, W_GN:W_GN + 1])
        mixer_out(S_HOUT, 2)

        ffn(S_FFN2, 1, 3)
        for j in range(8):
            split(S_KV + j + 4, 0, WHOLE)
        ffn(S_FFN3, 2, 4)

        act.wait_ge(bias_widened, 16)
        act.dma_start(bias[:], bass.AP(bias_wide, P - 1, [[H * (T + P) - 1, P], [T + P, H], [1, T]])
                      ).then_inc(bias_landed, 16)

        def exps(h):
            act.wait_ge(nmx_ready, h + 1)
            if h >= 2:
                act.wait_ge(rl_ready, h - 1)
            for m in range(2):
                for blk, (a, b) in enumerate(((0, P), (P, NS))):
                    j = 2 * m + blk
                    ins = A(sc[:, h % 2, m, a:b], sc[:, h % 2, m, a:b], ACT.Exp, bias=neg_mx(h)[:, j:j + 1],
                            accum_out=p_sum(h)[:, j:j + 1])
            ins.then_inc(exp_ready, 1)

        def o_rows(p):
            act.wait_ge(o_done, HP + p + 1)
            if p:
                act.wait_ge(oT_done, HP + p)
                o_high(1, HP + p, p - 1, sub_w)
            for tb in range(TB):
                for head in range(2):
                    ins = A(o_sb[:, tb, head, :], banks[6 + p % 2][:, (2 * tb + head) * P:(2 * tb + head + 1) * P],
                            ACT.Copy, scale=p_r1(2 * p + head)[:, tb:tb + 1])
            ins.then_inc(o_ready, 1)
            o_square(HP + p + 1)

        split(S_DIFF + 4, 0, WHOLE)
        split(S_DIFF + 5, 0, WHOLE)
        exps(0)
        split(S_DIFF + 6, 0, WHOLE)
        for h in range(H):
            if h + 1 < H:
                exps(h + 1)
            act.wait_ge(pT_done, h + 1)
            A(p_T[:, h % 2, :], banks[4][:, 0:NS], ACT.Copy).then_inc(pT_ready, 1)
            if h % 2 and h >= 3:
                o_rows(h // 2 - 1)
        split(S_DIFF + 7, 0, WHOLE)
        o_rows(HP - 1)
        o_high(1, 2 * HP, HP - 1, sub_w)
        mixer_out(S_DOUT, 5)
        ffn(S_FFN4, 3, 6)
        act.wait_ge(y_turned, 1)
        act.wait_ge(rstd_ready, 7)
        for half in range(2):
            A(y_rows[:, 0, half * 512:(half + 1) * 512], banks[half][:], ACT.Copy, scale=r_col[:, 0:1]).then_inc(y_ready[0], 1)

    @block.vector
    def _(dve):
        V = nc.vector

        def split(s, i, lots):
            for b, (k0, kc) in enumerate(lots):
                split_lot(2 * s + b, i, k0, kc)

        def split_lot(m, i, k0, kc):
            s = m // 2
            dve.wait_ge(hi_split, m + 1 + 8 * i)
            V.tensor_tensor(w_lo[:, s % RING, k0:k0 + kc, :], raw[:, m % LOTS, 0:kc, :],
                            w_hi[:, s % RING, k0:k0 + kc, :].bitcast(F32), ALU.subtract).then_inc(lo_split, 1)

        def x_low(r, c, i=0, f=1):
            cc = c + f * i
            if r == 3:
                dve.wait_ge(kxh_ready, c + 1 + f * i)
                V.scalar_tensor_tensor(kx_lo[:, ds(cc, 1), :], resid[:, ds(cc, 1), :], cols[:, ds(cc + W_KV, 1)],
                                       kx_hi[:, ds(cc, 1), :].bitcast(F32), ALU.mult, ALU.subtract).then_inc(kxl_ready, 1)
            dve.wait_ge(xh_ready, 8 * r + c + 1 + f * i)
            V.scalar_tensor_tensor(x_lo[:, ds(cc, 1), :], resid[:, ds(cc, 1), :], cols[:, ds(cc + W_NORM[r], 1)],
                                   x_hi[:, ds(cc, 1), :].bitcast(F32), ALU.mult, ALU.subtract).then_inc(xl_ready, 1)

        def bcast(ap):
            return ap[:].unsqueeze(1).to_broadcast([P, 2, T])

        def pair_ap(ap):
            return ap.rearrange("p (c t) -> p c t", c=2)

        def ms(r):
            dve.wait_ge(stat_done, r + 1)
            V.tensor_scalar(m_sq, banks[4][:, 0:2] if r else m_sq, 1.0 / D, EPS, ALU.mult, ALU.add).then_inc(ms_ready, 1)

        def diagonal(r):
            dve.wait_ge(rstd_ready, r + 1)
            for tb in range(TB):
                ins = V.tensor_scalar(diag[:, tb * P:(tb + 1) * P], ident[:], r_col[:, tb:tb + 1], None, ALU.mult)
            ins.then_inc(diag_ready, 1)

        def rb_copy(r):
            dve.wait_ge(rb_done, r + 1)
            V.tensor_copy(rstd_b[:], banks[5][:, 0:T]).then_inc(rb_ready, 1)

        def ffn(base, f, r_in, r_out, stats, n_rb):
            def pair(s, i, p, lots_g=WHOLE, lots_u=WHOLE, first=False):
                if first and stats:
                    if r_in:
                        ms(r_in)
                        diagonal(r_in)
                    rb_copy(r_in)
                    dve.wait_ge(rb_ready, n_rb)
                dve.wait_ge(slab_used, s + 1 + 4 * i)
                g_bank, u_bank = fh(p)
                V.tensor_tensor(pair_ap(gate_s[:, p % 2, :]), pair_ap(banks[g_bank][:]), bcast(rstd_b),
                                ALU.mult).then_inc(gate_scaled, 1)
                split(s + 4, i, lots_g)
                dve.wait_ge(slab_used, s + 2 + 4 * i)
                dve.wait_ge(silu_ready, NP_IN * f + p + 1 + 2 * i)
                V.tensor_tensor(gate_s[:, p % 2, :], gate_s[:, p % 2, :], banks[u_bank][:],
                                ALU.mult).then_inc(hid_ready, 1)
                split(s + 5, i, lots_u)
                dve.wait_ge(hidh_ready, NP_IN * f + p + 1 + 2 * i)
                hh = h_hi[:, ds(2 * p + 4 * i, 2), :]
                V.tensor_tensor(h_lo[:, ds(2 * p + 4 * i, 2), :], pair_ap(gate_s[:, p % 2, :]), hh.bitcast(F32),
                                ALU.subtract).then_inc(hidl_ready, 1)

            pair(base, 0, 0, first=True)
            with dve.Fori(0, 4) as i:
                pair(base + 2, i, 1)
                pair(base + 4, i, 2)
            pair(base + 18, 0, 9, QUARTERS[0][1], QUARTERS[1][1])
            pair(base + 20, 0, 10, QUARTERS[2][1], QUARTERS[3][1])
            sb = base + 2 * NP_IN

            def chunk(s, c, g, done):
                done()
                V.scalar_tensor_tensor(half_out[:, g, :], banks[4 + c % 4][:, 0:T], 0.5, rstd_b[:], ALU.mult,
                                       ALU.mult).then_inc(half_ready, 1)
                dve.wait_ge(half_ready, 8 * f + c + 1)
                V.tensor_tensor(resid[:, c, :], resid[:, c, :], half_out[:, g, :], ALU.add).then_inc(resid_ready, 1)
                if r_out < 6:
                    x_low(r_out, c)
                else:
                    dve.wait_ge(resid_ready, 8 * r_out + c + 1)
                    V.tensor_scalar(y_w[:, c, :], resid[:, c, :], cols[:, W_NORM[6] + c:W_NORM[6] + c + 1], None,
                                    ALU.mult).then_inc(yw_ready, 1)

            for dp in range(NP_OUT):
                s = sb + 4 * dp
                nxt = [(q, s + 4 + q, QUARTERS[q][1] if dp < NP_OUT - 1 else WHOLE) for q in range(4)]
                for q, ns, lots in nxt[:3]:
                    if ns < S_END:
                        split(ns, 0, lots)
                chunk(s, 2 * dp, 0, lambda: dve.wait_ge(even_done, NP_OUT * (r_out - 1) + dp + 1))
                chunk(s, 2 * dp + 1, 1, lambda: dve.wait_ge(slab_used, s + 4))
                if nxt[3][1] < S_END:
                    split(nxt[3][1], 0, nxt[3][2])

        def mixer_out(base, m, r_out):
            for c in range(KD):
                if c % 2 == 0:
                    dve.wait_ge(even_done, NP_OUT * (r_out - 1) + c // 2 + 1)
                else:
                    dve.wait_ge(slab_used, base + c // 2 + 1)
                V.tensor_tensor(resid[:, c, :], resid[:, c, :], banks[out_bank(m, c)][:, 0:T], ALU.add).then_inc(resid_ready, 1)
                if c not in (0, KD - 2):
                    x_low(r_out, c - 1)
                if c == KD - 3:
                    x_low(r_out, c)
                    split(base + RING, 0, WHOLE)
            x_low(r_out, KD - 1)
            for q in range(1, RING):
                split(base + RING + q, 0, WHOLE)

        def o_norm(n):
            dve.wait_ge(osq_ready, n)
            V.tensor_reduce(o_ss.rearrange("p (b h) -> p b h", b=TB), o_sq[:], AX_X, ALU.add).then_inc(oss_ready, 1)
            dve.wait_ge(oss_ready, n)
            V.tensor_scalar(o_ms, o_ss, 1.0 / P, EPS, ALU.mult, ALU.add).then_inc(oms_ready, 1)

        def o_scale(n, gated):
            dve.wait_ge(ors_ready, n)
            rs = o_rs.unsqueeze(2).to_broadcast([P, 4, P])
            flat = o_sb[:].rearrange("p b h e -> p (b h) e")
            V.tensor_tensor(flat, flat, rs, ALU.mult).then_inc(on_step, 1)
            if gated:
                dve.wait_ge(on_step, 2 * n - 1)
                V.tensor_tensor(o_sb[:].rearrange("p b h e -> p b (h e)"), o_sb[:].rearrange("p b h e -> p b (h e)"),
                                hgate[:], ALU.mult).then_inc(on_step, 1)

        def o_low(m, n, p, w):
            dve.wait_ge(oh_ready, n)
            V.scalar_tensor_tensor(h_lo[:, ds(2 * p, 2), :], pair_ap(turn_bank(m)[:]), w,
                                   h_hi[:, ds(2 * p, 2), :].bitcast(F32), ALU.mult, ALU.subtract).then_inc(ol_ready, 1)

        def resid_chunks(j):
            dve.wait_ge(x_turned, j + 1)
            for c in (2 * j, 2 * j + 1):
                V.tensor_copy(resid[:, c, :], banks[4 + j][:, (c % 2) * T:(c % 2 + 1) * T]).then_inc(resid_ready, 2)

        resid_chunks(0)
        dve.wait_ge(vec_turned, 1)
        V.tensor_copy(cols[:], banks[0][:, 0:NCOL]).then_inc(cols_ready, 1)
        dve.wait_ge(cols_ready, 1)
        x_low(0, 0)
        x_low(0, 1)
        resid_chunks(2)
        split_lot(0, 0, 0, 4)
        x_low(0, 2)
        x_low(0, 3)
        x_low(0, 4)
        x_low(0, 5)
        split_lot(1, 0, 4, 4)
        x_low(0, 6)
        x_low(0, 7)
        ms(0)
        for s in range(1, 4):
            split(s, 0, WHOLE)
            if s == 1:
                diagonal(0)
                dve.wait_ge(brow_done, 1)
                V.tensor_copy(bias_rows[:, 0:T], banks[3][0:H, 0:T]).then_inc(brow_ready, 1)
        lbr = cols[:, W_LB:W_LB + 2 * KD].rearrange("p (l c) -> p l c", l=2)
        V.tensor_tensor(lb, lbr[:, 0, :], lbr[:, 1, :], ALU.max).then_inc(lb_step, 1)
        dve.wait_ge(lb_step, 1)
        V.tensor_tensor(lb_tmp[:, 0:2, :], lbr, lb.unsqueeze(1).to_broadcast([P, 2, KD]), ALU.subtract).then_inc(lb_step, 1)
        dve.wait_ge(lam_landed, 16)
        for j in range(2):
            ins = V.tensor_tensor_reduce(out=lam_rows[:, 2 * j, :], in0=lam_rows[:, 2 * j, :], in1=lam_rows[:, 2 * j + 1, :],
                                         scale=1.0, scalar=0.0, op0=ALU.mult, op1=ALU.add, accum_out=lam4[:, j:j + 1])
        ins.then_inc(lam_dot, 1)
        dve.wait_ge(lb_exp, 1)
        V.tensor_tensor(om_lb, lb_tmp[:, 2, :], lb_tmp[:, 3, :], ALU.add).then_inc(lb_step, 1)
        dve.wait_ge(lb_step, 3)
        V.reciprocal(lb, om_lb).then_inc(lb_step, 1)
        dve.wait_ge(lb_step, 4)
        V.tensor_tensor(lb, lb, lb_tmp[:, 2, :], ALU.mult).then_inc(lb_step, 1)
        dve.wait_ge(lb_step, 5)
        V.tensor_scalar(om_lb, lb, -1.0, 1.0, ALU.mult, ALU.add).then_inc(lb_step, 1)
        dve.wait_ge(lam_exp, 1)
        V.tensor_tensor(neg_lam, lam4[:, 3:4], lam4[:, 2:3], ALU.subtract).then_inc(lam_step, 1)
        dve.wait_ge(lam_step, 1)
        V.tensor_scalar(neg_lam, neg_lam, -LAMBDA_INIT, None, ALU.add).then_inc(lam_step, 1)
        V.tensor_scalar(sub_w, cols[:, W_SUB:W_SUB + 1], 1.0 - LAMBDA_INIT, None, ALU.mult).then_inc(lam_step, 1)

        ffn(S_FFN1, 0, 0, 1, True, 1)

        dve.wait_ge(hg_landed, 32)
        dve.wait_ge(lb_step, 6)
        dve.wait_ge(bias_stored, 16)
        dve.wait_ge(aT_zeroed, 1)

        def by_chunk(ap):
            return ap[:].rearrange("p h (c j) -> p (h c) j", j=CHUNK)

        def a_evac(n):
            dve.wait_ge(coreA_done, n + 1)
            V.tensor_copy(kd_rows[:].rearrange("p b h e -> p (b h e)"), banks[4][:]).then_inc(kdr_ready, 1)
            V.copy_predicated(a_T[:].rearrange("p h b e -> p (h b) e"),
                              causal[:].bitcast(U32).unsqueeze(1).to_broadcast([P, 4, P]),
                              banks[5][:].rearrange("p (j e) -> p j e", j=4)).then_inc(aT_ready, 1)

        def b_evac(n):
            dve.wait_ge(coreB_done, n + 1)
            for head in range(2):
                V.tensor_copy(state[:, head, 0, :], u_of(head, 0)).then_inc(st_ready, 1)
            for c in (1, 2):
                for head in range(2):
                    dve.wait_ge(st_ready, 6 * n + 2 * c + head - 1)
                    V.scalar_tensor_tensor(state[:, head, c, :], state[:, head, c - 1, :],
                                           e0[:, head, c * CHUNK + CHUNK - 1:c * CHUNK + CHUNK],
                                           u_of(head, c), ALU.mult, ALU.add).then_inc(st_ready, 1)

        def c_evac(n):
            dve.wait_ge(o_done, n + 1)
            V.tensor_copy(o_sb[:].rearrange("p b h e -> p (b h e)"), banks[4][:]).then_inc(o_ready, 1)

        def head_pair(s, i, prev, first):
            n = i + (0 if first else prev + 1)
            pv = None if first else i + prev
            if first:
                ms(1)
                diagonal(1)
                rb_copy(1)
                dve.wait_ge(rb_ready, 2)
            dve.wait_ge(slab_used, s + 1 + 4 * i)
            V.tensor_tensor(fr[:], pair_ap(banks[0][:]), bcast(rstd_b), ALU.mult).then_inc(fr_ready, 1)
            split(s + 4, i, WHOLE)
            if not first:
                a_evac(pv)
            dve.wait_ge(slab_used, s + 2 + 4 * i)
            V.tensor_tensor(qr[:], pair_ap(banks[1][:]), bcast(rstd_b), ALU.mult).then_inc(qr_ready, 1)
            split(s + 5, i, WHOLE)
            if not first:
                b_evac(pv)
            dve.wait_ge(fsig_ready, n + 1)
            for head in range(2):
                hc = 2 * n + head
                ins = V.tensor_scalar(fg[:, head, :], fg[:, head, :], small[:, ds(hc + 16, 1)], small[:, ds(hc + 8, 1)],
                                      ALU.mult, ALU.add)
            ins.then_inc(f_ready, 1)
            dve.wait_ge(f_ready, n + 1)
            V.tensor_scalar(kk[:], fg[:], -1.0, 1.0, ALU.mult, ALU.add).then_inc(k_ready, 1)
            dve.wait_ge(lg_ready, n + 1)
            V.tensor_tensor_scan(bc[:].rearrange("p h t -> p (h t)"), resets[:], lg[:].rearrange("p h t -> p (h t)"),
                                 0.0, ALU.mult, ALU.add).then_inc(bc_ready, 1)
            dve.wait_ge(bc_ready, n + 1)
            b3 = by_chunk(bc)
            V.tensor_tensor(by_chunk(dm), b3, b3[:, :, CHUNK // 2 - 1:CHUNK // 2].to_broadcast([P, 8, CHUNK]), ALU.subtract)
            V.tensor_tensor(by_chunk(dl), b3[:, :, CHUNK - 1:CHUNK].to_broadcast([P, 8, CHUNK]), b3, ALU.subtract).then_inc(d_ready, 1)
            if not first:
                c_evac(pv)
            dve.wait_ge(slab_used, s + 3 + 4 * i)
            for tb in range(TB):
                ins = V.tensor_scalar(hv[:, tb, :], banks[2][:, tb * 256:(tb + 1) * 256], r_col[:, tb:tb + 1], None, ALU.mult)
            ins.then_inc(hv_ready, 1)
            if not first:
                o_norm(pv + 1)
            dve.wait_ge(e_ready, 4 * n + 1)
            dve.wait_ge(k_ready, n + 1)
            V.tensor_tensor(ki[:], kk[:], e2[:], ALU.mult).then_inc(ki_ready, 1)
            if not first:
                o_scale(pv + 1, True)
            split(s + 6, i, WHOLE)
            split(s + 7, i, WHOLE)
            dve.wait_ge(gsig_ready, n + 1)
            for tb in range(TB):
                ins = V.scalar_tensor_tensor(hgate[:, tb, :], banks[3][:, tb * 256:(tb + 1) * 256], r_col[:, tb:tb + 1],
                                             hgate[:, tb, :], ALU.mult, ALU.mult)
            ins.then_inc(hgate_ready, 1)
            if not first:
                o_low(0, pv + 1, pv, cols[:, W_GN:W_GN + 1])

        head_pair(S_HGRN, 0, -1, True)
        with dve.Fori(0, HP - 1) as i:
            head_pair(S_HGRN + 4, i, 0, False)
        last = HP - 1
        a_evac(last)
        b_evac(last)
        c_evac(last)
        o_norm(HP)
        dve.wait_ge(hgate_ready, HP)
        o_scale(HP, True)
        o_low(0, HP, last, cols[:, W_GN:W_GN + 1])
        mixer_out(S_HOUT, 0, 2)

        ffn(S_FFN2, 1, 2, 3, True, 3)

        ms(3)
        diagonal(3)
        rb_copy(3)
        dve.wait_ge(rb_ready, 4)
        for j in range(8):
            dve.wait_ge(slab_used, S_KV + j + 1)
            if j < 4:
                V.tensor_tensor(k_T[:, 2 * j:2 * j + 2, :], pair_ap(banks[kv_bank(j)][:]), bcast(rstd_b), ALU.mult).then_inc(kv_ready, 1)
            else:
                for tb in range(TB):
                    ins = V.tensor_scalar(v_all[:, tb, (j - 4) * 256:(j - 3) * 256], banks[kv_bank(j)][:, tb * 256:(tb + 1) * 256],
                                          r_col[:, tb:tb + 1], None, ALU.mult)
                ins.then_inc(kv_ready, 1)
            split(S_KV + j + 4, 0, WHOLE)

        ffn(S_FFN3, 2, 3, 4, False, 4)

        def add_bias(h):
            dve.wait_ge(sc_done, h + 1)
            if h >= 2:
                dve.wait_ge(pr_ready, 2 * (h - 1))
            for m in range(2):
                for blk, (a, b) in enumerate(((0, P), (P, NS))):
                    j = 2 * m + blk
                    V.tensor_tensor_reduce(out=sc[:, h % 2, m, a:b], in0=banks[2 * (h % 2) + m][:, a:b],
                                           in1=bias[:, h, P - a:T], scale=1.0, scalar=MASKED, op0=ALU.add, op1=ALU.max,
                                           accum_out=neg_mx(h)[:, j:j + 1]).then_inc(sc_ready, 1)
            dve.wait_ge(sc_ready, 4 * (h + 1))
            V.tensor_scalar(neg_mx(h), neg_mx(h), -1.0, None, ALU.mult).then_inc(nmx_ready, 1)

        def q_evac(j):
            n = (0, HP, 2, HP + 2)[j]
            dve.wait_ge(slab_used, S_DIFF + j + 1)
            V.scalar_tensor_tensor(q_T[:, n:n + 2, :], pair_ap(banks[q_bank(j)][:]), DH ** -0.5, bcast(rstd_b),
                                   ALU.mult, ALU.mult).then_inc(qT_ready, 1)

        ms(4)
        diagonal(4)
        rb_copy(4)
        dve.wait_ge(rb_ready, 5)
        q_evac(0)
        split(S_DIFF + 4, 0, WHOLE)
        q_evac(1)
        split(S_DIFF + 5, 0, WHOLE)
        dve.wait_ge(bias_landed, 16)
        add_bias(0)
        dve.wait_ge(lam_step, 3)
        for h in range(H):
            if h + 1 < H:
                add_bias(h + 1)
            dve.wait_ge(exp_ready, h + 1)
            V.reciprocal(p_r1(h), p_sum(h)[:, 0:2])
            V.reciprocal(p_r2, p_sum(h)[:, 2:4]).then_inc(rcp_ready, 1)
            dve.wait_ge(rcp_ready, h + 1)
            V.scalar_tensor_tensor(p_rl, p_sum(h)[:, 0:2], neg_lam, p_r2, ALU.mult, ALU.mult).then_inc(rl_ready, 1)
            dve.wait_ge(rl_ready, h + 1)
            for blk, (a, b) in enumerate(((0, P), (P, NS))):
                V.scalar_tensor_tensor(pr[:, h % 2, a:b], sc[:, h % 2, 1, a:b], p_rl[:, blk:blk + 1],
                                       sc[:, h % 2, 0, a:b], ALU.mult, ALU.add).then_inc(pr_ready, 1)
            if h % 2 and h >= 5:
                o_scale(HP + h // 2 - 1, False)
            if h < 2:
                q_evac(2 + h)
            if h == 0:
                split(S_DIFF + 6, 0, WHOLE)
            if h % 2 == 0 and h >= 4:
                if h >= 6:
                    o_low(1, HP + h // 2 - 2, h // 2 - 3, sub_w)
                o_norm(HP + h // 2 - 1)
        o_low(1, 2 * HP - 2, HP - 3, sub_w)
        o_norm(2 * HP - 1)
        split_lot(2 * (S_DIFF + 7), 0, *WHOLE[0])
        o_scale(2 * HP - 1, False)
        split_lot(2 * (S_DIFF + 7) + 1, 0, *WHOLE[1])
        o_low(1, 2 * HP - 1, HP - 2, sub_w)
        o_norm(2 * HP)
        o_scale(2 * HP, False)
        o_low(1, 2 * HP, HP - 1, sub_w)
        mixer_out(S_DOUT, 1, 5)

        ffn(S_FFN4, 3, 5, 6, True, 6)
        ms(6)
        dve.wait_ge(y_turned, 1)
        dve.wait_ge(rstd_ready, 7)
        for half in range(2):
            V.tensor_scalar(y_rows[:, 1, half * 512:(half + 1) * 512], banks[2 + half][:], r_col[:, 1:2], None,
                            ALU.mult).then_inc(y_ready[1], 1)

    @block.gpsimd
    def _(pool):
        G = nc.gpsimd
        G.memset(ones[:], 1.0).then_inc(ones_set, 1)
        G.memset(neg_half, -0.5).then_inc(neg_set, 1)
        G.memset(bias_rows[:, T:T + P], MASKED).then_inc(brow_set, 1)
        G.memset(a_T[:], 0.0).then_inc(aT_zeroed, 1)
        pool.wait_ge(neg_set, 1)

        def stats(r):
            before = (2 * KD - 1) * (r - 1)

            def squares(dst, c, chunk):
                pool.wait_ge(resid_ready, chunk + 8 * r + 1)
                G.tensor_tensor(dst[:], resid[:, c, :], resid[:, c, :], ALU.mult).then_inc(sumsq_step, 1)

            def add(wait):
                pool.wait_ge(sumsq_step, wait)
                G.tensor_tensor(sumsq[:], sumsq[:], square[:], ALU.add).then_inc(sumsq_step, 1)

            pool.wait_ge(stat_done, r)
            squares(sumsq, 0, 0)
            squares(square, 1, 1)
            with pool.Fori(2, KD) as c:
                add(c * 2 + before - 2)
                pool.wait_ge(sumsq_step, c * 2 + before - 1)
                squares(square, ds(c, 1), c)
            if r < 6:
                add(before + 2 * KD - 2)
            pool.wait_ge(ms_ready, r + 1)
            G.tensor_tensor(r_col, m_sq, neg_half[:, 0:2], ALU.pow).then_inc(rstd_ready, 1)

        def o_rstd(n):
            pool.wait_ge(oms_ready, n)
            G.tensor_tensor(o_rs, o_ms, neg_half, ALU.pow).then_inc(ors_ready, 1)

        def head_pair(n, prev):
            pool.wait_ge(qsig_ready, n + 1)
            if prev is not None:
                pool.wait_ge(qe_ready, prev + 1)
            G.tensor_tensor(qq[:], qr[:], sg[:], ALU.mult).then_inc(q_ready, 1)
            pool.wait_ge(e_ready, 4 * n + 2)
            pool.wait_ge(k_ready, n + 1)
            if prev is not None:
                pool.wait_ge(coreA_done, prev + 1)
            G.tensor_tensor(kd[:], kk[:], e3[:], ALU.mult)
            pool.wait_ge(e_ready, 4 * n + 3)
            pool.wait_ge(q_ready, n + 1)
            G.tensor_tensor(qi[:], qq[:], e1[:], ALU.mult).then_inc(kqi_ready, 1)
            pool.wait_ge(e_ready, 4 * n + 4)
            if prev is not None:
                o_rstd(prev + 1)
            G.tensor_tensor(qe[:], qq[:], e0[:], ALU.mult).then_inc(qe_ready, 1)

        pool.wait_ge(ms_ready, 1)
        G.tensor_tensor(r_col, m_sq, neg_half[:, 0:2], ALU.pow).then_inc(rstd_ready, 1)
        stats(1)
        head_pair(0, None)
        with pool.Fori(1, HP) as n:
            head_pair(n, n - 1)
        o_rstd(HP)
        for r in (2, 3, 4):
            stats(r)
        for p in range(HP):
            o_rstd(HP + p + 1)
        stats(5)
        stats(6)

    block.__exit__(None, None, None)


_INS = ["x", "norm_w", "ffn_w_in", "ffn_w_out", "hgrn_w_in", "hgrn_lower_bounds", "hgrn_gnorm_w", "hgrn_w_out",
        "kv_norm_w", "w_kv", "rel_bias", "diff_w_q", "diff_lambda", "diff_subln_w", "diff_w_out", "final_norm_w"]


def kernel(**inputs):
    import concourse.bacc as _bacc
    from concourse.bass_utils import run_bass_kernel_spmd as _run

    nc = _bacc.Bacc("TRN2", target_bir_lowering=False, num_devices=1)
    arrays, args = {}, []
    given = {name: np.ascontiguousarray(inputs[name]) for name in _INS}
    given.update(shape_constants(given["x"].shape[1]))
    for name, a in given.items():
        arrays[f"in_{name}"] = a
        args.append(nc.dram_tensor(f"in_{name}", a.shape, mybir.dt.from_np(a.dtype), kind="ExternalInput").ap())
    shape = given["x"].shape
    args.append(nc.dram_tensor("out_y", shape, F32, kind="ExternalOutput").ap())
    trunk(nc, *args)
    r = _run(nc, [arrays], core_ids=[0])
    return r.results[0]["out_y"]
```
